# Optimizing a Trainium2 kernel written in Bass

```python
import math
import jax, jax.numpy as jnp
from jax import lax
import numpy as np

D_MODEL = 1024
BATCH = 1
SEQ = 256
DEPTH = 1
DEC_BATCH = 1
DEC_SEQ = 32
PAST_LEN = 512

CHUNK = 64
Q_BLOCK = 128
D_INNER = 2 * D_MODEL
SSM_HEAD_DIM = 64
SSM_HEADS = D_INNER // SSM_HEAD_DIM
SSM_GROUPS = 8
HEADS_PER_GROUP = SSM_HEADS // SSM_GROUPS
SSM_STATE = 128
CONV_WIDTH = 4
CONV_DIM = D_INNER + 2 * SSM_GROUPS * SSM_STATE
MLA_HEADS = 16
QK_NOPE = 128
QK_ROPE = 64
V_HEAD = 128
Q_RANK = 512
KV_RANK = 512
ROPE_THETA = 10000.0
ATTN_SCALE = (QK_NOPE + QK_ROPE) ** -0.5
D_FF = 4 * D_MODEL
RMS_EPS = 1e-6
LN_EPS = 1e-5
ALPHA = (2 * DEPTH) ** 0.25
BETA = (8 * DEPTH) ** -0.25
IN_SPLITS = [2 * D_MODEL,
             2 * D_MODEL + D_INNER,
             2 * D_MODEL + D_INNER + CONV_DIM,
             2 * D_MODEL + D_INNER + CONV_DIM + SSM_HEADS,
             2 * D_MODEL + D_INNER + CONV_DIM + SSM_HEADS + Q_RANK]
IN_COLS = 2 * D_MODEL + D_INNER + CONV_DIM + SSM_HEADS + Q_RANK + KV_RANK + QK_ROPE

kernel_name = 'hybrid_ssd_mla_deepnorm_stream_step'

def _rmsnorm(t):
    tf = t.astype(jnp.float32)
    return (tf * lax.rsqrt(jnp.mean(tf * tf, axis=-1, keepdims=True) + RMS_EPS)).astype(t.dtype)

def _layernorm(t, g, b):
    tf = t.astype(jnp.float32)
    mu = jnp.mean(tf, axis=-1, keepdims=True)
    var = jnp.mean(jnp.square(tf - mu), axis=-1, keepdims=True)
    return ((tf - mu) * lax.rsqrt(var + LN_EPS)).astype(t.dtype) * g + b

def _rope(t, pos):
    inv = ROPE_THETA ** (-jnp.arange(0, QK_ROPE, 2, dtype=jnp.float32) / QK_ROPE)
    ang = pos.astype(jnp.float32)[:, None] * inv[None, :]
    cos = jnp.cos(ang)[None, :, None, :].astype(t.dtype)
    sin = jnp.sin(ang)[None, :, None, :].astype(t.dtype)
    t1, t2 = jnp.split(t, 2, axis=-1)
    return jnp.concatenate([t1 * cos - t2 * sin, t1 * sin + t2 * cos], axis=-1)

def _causal_conv(xbc, conv_state, conv_w, conv_b):
    L = xbc.shape[1]
    xp = jnp.concatenate([conv_state, xbc], axis=1)
    out = conv_b + sum(xp[:, k:k + L] * conv_w[k] for k in range(CONV_WIDTH))
    return jax.nn.silu(out), xp[:, L:]

def _ssd(xh, dt, a, bm, cm, s0, chunk):
    bsz, L = xh.shape[:2]
    nc = L // chunk

    def blocks(t):
        return jnp.moveaxis(t.reshape(bsz, nc, chunk, *t.shape[2:]), 1, 0)

    causal = jnp.tril(jnp.ones((chunk, chunk), dtype=bool))[None, :, :, None, None]

    def step(s, inp):
        xc, dtc, bc, cc = inp
        dtype = xc.dtype
        acum = jnp.cumsum((dtc * a).astype(jnp.float32), axis=1)
        seg = jnp.where(causal, acum[:, :, None] - acum[:, None, :], -jnp.inf)
        xdt = xc * dtc[..., None]
        cb = jnp.einsum('bign,bjgn->bijg', cc, bc)
        y = jnp.einsum('bijg,bijgr,bjgrp->bigrp', cb, jnp.exp(seg).astype(dtype), xdt)
        y = y + jnp.einsum('bign,bgrpn->bigrp', cc, s) * jnp.exp(acum).astype(dtype)[..., None]
        w_end = jnp.exp(acum[:, -1:] - acum).astype(dtype)
        s_new = (s * jnp.exp(acum[:, -1]).astype(dtype)[..., None, None]
                 + jnp.einsum('bjgr,bjgn,bjgrp->bgrpn', w_end, bc, xdt))
        return s_new.astype(s.dtype), y

    s_fin, ys = lax.scan(step, s0, (blocks(xh), blocks(dt), blocks(bm), blocks(cm)))
    return jnp.moveaxis(ys, 0, 1).reshape(xh.shape), s_fin

def _mla_attend(q_nope, q_pe, ckv, kpe, w_uk, w_uv, q_pos, k_pos):
    q_lat = jnp.einsum('bqhd,chd->bqhc', q_nope, w_uk)
    s = (jnp.einsum('bqhc,bkc->bhqk', q_lat, ckv)
         + jnp.einsum('bqhr,bkr->bhqk', q_pe, kpe)).astype(jnp.float32) * ATTN_SCALE
    mask = (k_pos[None, :] // CHUNK) <= (q_pos[:, None] // CHUNK)
    p = jax.nn.softmax(jnp.where(mask[None, None], s, -jnp.inf), axis=-1).astype(ckv.dtype)
    o_lat = jnp.einsum('bhqk,bkc->bqhc', p, ckv)
    return jnp.einsum('bqhc,chv->bqhv', o_lat, w_uv)

def _layer(x, pos0, lp, past):
    bsz, L, _ = x.shape
    dtype = x.dtype
    proj = x @ lp['w_in']
    gate_pre, z, xbc, dt_raw, q_a, kv_a = jnp.split(proj, IN_SPLITS, axis=-1)
    g_ssm, g_mla = jnp.split(jax.nn.sigmoid(gate_pre + lp['b_gate']), 2, axis=-1)
    pos = pos0 + jnp.arange(L, dtype=jnp.int32)

    if past is None:
        conv_state = jnp.zeros((bsz, CONV_WIDTH - 1, CONV_DIM), dtype)
        s0 = jnp.zeros((bsz, SSM_GROUPS, HEADS_PER_GROUP, SSM_HEAD_DIM, SSM_STATE), dtype)
        chunk = CHUNK
    else:
        conv_state = past['conv']
        s0 = past['ssm'].reshape(bsz, SSM_GROUPS, HEADS_PER_GROUP, SSM_HEAD_DIM, SSM_STATE)
        chunk = L
    xbc, conv_new = _causal_conv(xbc, conv_state, lp['conv_w'], lp['conv_b'])
    xs, bm, cm = jnp.split(xbc, [D_INNER, D_INNER + SSM_GROUPS * SSM_STATE], axis=-1)
    xh = xs.reshape(bsz, L, SSM_GROUPS, HEADS_PER_GROUP, SSM_HEAD_DIM)
    bm = bm.reshape(bsz, L, SSM_GROUPS, SSM_STATE)
    cm = cm.reshape(bsz, L, SSM_GROUPS, SSM_STATE)
    dt = jax.nn.softplus(dt_raw + lp['dt_bias']).reshape(bsz, L, SSM_GROUPS, HEADS_PER_GROUP)
    a = -jnp.exp(lp['a_log']).reshape(SSM_GROUPS, HEADS_PER_GROUP)
    yh, s_fin = _ssd(xh, dt, a, bm, cm, s0, chunk)
    yh = yh + xh * lp['d_skip'].reshape(SSM_GROUPS, HEADS_PER_GROUP, 1)
    yg = (yh.reshape(bsz, L, D_INNER) * jax.nn.silu(z)).reshape(bsz, L, SSM_GROUPS, D_INNER // SSM_GROUPS)
    yg = _rmsnorm(yg).reshape(bsz, L, D_INNER) * lp['ssm_norm_g']
    y_ssm = yg @ lp['w_ssm_proj']

    q = ((_rmsnorm(q_a) * lp['q_norm_g']) @ lp['w_q_b']).reshape(bsz, L, MLA_HEADS, QK_NOPE + QK_ROPE)
    q_nope, q_pe = jnp.split(q, [QK_NOPE], axis=-1)
    q_pe = _rope(q_pe, pos)
    ckv, kpe = jnp.split(kv_a, [KV_RANK], axis=-1)
    ckv = _rmsnorm(ckv) * lp['kv_norm_g']
    kpe = _rope(kpe[:, :, None, :], pos)[:, :, 0, :]
    if past is None:
        def block(i):
            q0 = i * Q_BLOCK
            return _mla_attend(lax.dynamic_slice_in_dim(q_nope, q0, Q_BLOCK, axis=1),
                               lax.dynamic_slice_in_dim(q_pe, q0, Q_BLOCK, axis=1),
                               ckv, kpe, lp['w_uk'], lp['w_uv'],
                               q0 + jnp.arange(Q_BLOCK, dtype=jnp.int32), pos)
        o = lax.map(block, jnp.arange(L // Q_BLOCK, dtype=jnp.int32))
        o = jnp.moveaxis(o, 0, 1).reshape(bsz, L, MLA_HEADS * V_HEAD)
    else:
        ckv_all = jnp.concatenate([past['ckv'], ckv], axis=1)
        kpe_all = jnp.concatenate([past['kpe'], kpe], axis=1)
        k_pos = jnp.arange(ckv_all.shape[1], dtype=jnp.int32)
        o = _mla_attend(q_nope, q_pe, ckv_all, kpe_all, lp['w_uk'], lp['w_uv'], pos, k_pos)
        o = o.reshape(bsz, L, MLA_HEADS * V_HEAD)
    y_mla = o @ lp['w_mla_proj']

    mix = (g_ssm * y_ssm + g_mla * y_mla) @ lp['w_out']
    h = _layernorm(ALPHA * x + mix, lp['ln1_g'], lp['ln1_b'])
    ff = jnp.square(jax.nn.relu(h @ lp['w_up'])) @ lp['w_down']
    y = _layernorm(ALPHA * h + ff, lp['ln2_g'], lp['ln2_b'])
    s_fin = s_fin.reshape(bsz, SSM_HEADS, SSM_HEAD_DIM, SSM_STATE)
    return y, ckv, kpe, s_fin, conv_new

def setup_inputs(seed: int = 0) -> dict:
    key = jax.random.key(seed)
    ks = jax.random.split(key, 32)
    f32 = jnp.float32
    nrm = lambda k, shape, s: jax.random.normal(k, shape, f32) * s
    dt0 = jnp.exp(jax.random.uniform(ks[8], (DEPTH, SSM_HEADS), f32) * (math.log(0.1) - math.log(0.001)) + math.log(0.001))
    return {
        'x_prompt': nrm(ks[0], (BATCH, SEQ, D_MODEL), 1.0),
        'x_sample': nrm(ks[1], (DEC_BATCH, DEC_SEQ, D_MODEL), 1.0),
        'cache_ckv': nrm(ks[2], (DEPTH, DEC_BATCH, PAST_LEN, KV_RANK), 1.0),
        'cache_kpe': nrm(ks[3], (DEPTH, DEC_BATCH, PAST_LEN, QK_ROPE), 1.0),
        'state_ssm': nrm(ks[4], (DEPTH, DEC_BATCH, SSM_HEADS, SSM_HEAD_DIM, SSM_STATE), 0.5),
        'state_conv': nrm(ks[5], (DEPTH, DEC_BATCH, CONV_WIDTH - 1, CONV_DIM), 1.0),
        'w_in': nrm(ks[6], (DEPTH, D_MODEL, IN_COLS), D_MODEL ** -0.5),
        'b_gate': nrm(ks[7], (DEPTH, 2 * D_MODEL), 0.02),
        'conv_w': nrm(ks[9], (DEPTH, CONV_WIDTH, CONV_DIM), CONV_WIDTH ** -0.5),
        'conv_b': nrm(ks[10], (DEPTH, CONV_DIM), 0.02),
        'dt_bias': dt0 + jnp.log(-jnp.expm1(-dt0)),
        'a_log': jnp.log(jax.random.uniform(ks[11], (DEPTH, SSM_HEADS), f32, 1.0, 16.0)),
        'd_skip': 1.0 + nrm(ks[12], (DEPTH, SSM_HEADS), 0.02),
        'ssm_norm_g': 1.0 + nrm(ks[13], (DEPTH, D_INNER), 0.02),
        'w_ssm_proj': nrm(ks[14], (DEPTH, D_INNER, D_MODEL), BETA * D_INNER ** -0.5),
        'q_norm_g': 1.0 + nrm(ks[15], (DEPTH, Q_RANK), 0.02),
        'w_q_b': nrm(ks[16], (DEPTH, Q_RANK, MLA_HEADS * (QK_NOPE + QK_ROPE)), Q_RANK ** -0.5),
        'kv_norm_g': 1.0 + nrm(ks[17], (DEPTH, KV_RANK), 0.02),
        'w_uk': nrm(ks[18], (DEPTH, KV_RANK, MLA_HEADS, QK_NOPE), KV_RANK ** -0.5),
        'w_uv': nrm(ks[19], (DEPTH, KV_RANK, MLA_HEADS, V_HEAD), BETA * KV_RANK ** -0.5),
        'w_mla_proj': nrm(ks[20], (DEPTH, MLA_HEADS * V_HEAD, D_MODEL), BETA * (MLA_HEADS * V_HEAD) ** -0.5),
        'w_out': nrm(ks[21], (DEPTH, D_MODEL, D_MODEL), BETA * D_MODEL ** -0.5),
        'ln1_g': 1.0 + nrm(ks[22], (DEPTH, D_MODEL), 0.02),
        'ln1_b': nrm(ks[23], (DEPTH, D_MODEL), 0.02),
        'w_up': nrm(ks[24], (DEPTH, D_MODEL, D_FF), BETA * D_MODEL ** -0.5),
        'w_down': nrm(ks[25], (DEPTH, D_FF, D_MODEL), BETA * D_FF ** -0.5),
        'ln2_g': 1.0 + nrm(ks[26], (DEPTH, D_MODEL), 0.02),
        'ln2_b': nrm(ks[27], (DEPTH, D_MODEL), 0.02),
    }

def reference(x_prompt, x_sample, cache_ckv, cache_kpe, state_ssm, state_conv,
              w_in, b_gate, conv_w, conv_b, dt_bias, a_log, d_skip, ssm_norm_g, w_ssm_proj,
              q_norm_g, w_q_b, kv_norm_g, w_uk, w_uv, w_mla_proj, w_out,
              ln1_g, ln1_b, w_up, w_down, ln2_g, ln2_b):
    yp, ys = x_prompt, x_sample
    st_p, st_s = [], []
    for i in range(DEPTH):
        lp = dict(w_in=w_in[i], b_gate=b_gate[i], conv_w=conv_w[i], conv_b=conv_b[i],
                  dt_bias=dt_bias[i], a_log=a_log[i], d_skip=d_skip[i], ssm_norm_g=ssm_norm_g[i],
                  w_ssm_proj=w_ssm_proj[i], q_norm_g=q_norm_g[i], w_q_b=w_q_b[i],
                  kv_norm_g=kv_norm_g[i], w_uk=w_uk[i], w_uv=w_uv[i], w_mla_proj=w_mla_proj[i],
                  w_out=w_out[i], ln1_g=ln1_g[i], ln1_b=ln1_b[i], w_up=w_up[i], w_down=w_down[i],
                  ln2_g=ln2_g[i], ln2_b=ln2_b[i])
        yp, ckv_p, kpe_p, ssm_p, conv_p = _layer(yp, 0, lp, None)
        past = dict(ckv=cache_ckv[i], kpe=cache_kpe[i], ssm=state_ssm[i], conv=state_conv[i])
        ys, ckv_s, kpe_s, ssm_s, conv_s = _layer(ys, PAST_LEN, lp, past)
        st_p.append((ckv_p, kpe_p, ssm_p, conv_p))
        st_s.append((ckv_s, kpe_s, ssm_s, conv_s))
    new_ckv_p = jnp.stack([t[0] for t in st_p])
    new_kpe_p = jnp.stack([t[1] for t in st_p])
    new_ssm_p = jnp.stack([t[2] for t in st_p])
    new_conv_p = jnp.stack([t[3] for t in st_p])
    new_ckv_s = jnp.stack([t[0] for t in st_s])
    new_kpe_s = jnp.stack([t[1] for t in st_s])
    new_ssm_s = jnp.stack([t[2] for t in st_s])
    new_conv_s = jnp.stack([t[3] for t in st_s])
    return (yp, ys, new_ckv_p, new_kpe_p, new_ssm_p, new_conv_p, new_ckv_s, new_kpe_s, new_ssm_s, new_conv_s)


_drawn_inputs = setup_inputs


def setup_inputs(seed=0):
    import zlib

    import numpy as np

    out = dict(_drawn_inputs(seed))
    spreads = {}
    factors = {'cache_ckv': 8.0,
     'cache_kpe': 8.0,
     'b_gate': 8.0,
     'd_skip': 200.0,
     'ssm_norm_g': 174.911,
     'q_norm_g': 8.0,
     'w_q_b': 4.914,
     'kv_norm_g': 2.97,
     'w_uk': 5.564,
     'w_uv': 3.835,
     'w_mla_proj': 3.92,
     'ln1_g': 7.642,
     'ln1_b': 7.837,
     'ln2_g': 21.64,
     'ln2_b': 24.186}
    for name, (base, spread) in spreads.items():
        noise = np.random.default_rng([zlib.crc32(name.encode()), seed]).standard_normal(out[name].shape)
        drawn = base * np.exp(spread * noise) if base else spread * noise
        out[name] = __import__('jax').numpy.asarray(drawn.astype(out[name].dtype))
    for name, factor in factors.items():
        out[name] = (out[name] * factor).astype(out[name].dtype)
    return out
```

```python
from contextlib import ExitStack

import concourse.bass as bass
from concourse import mybir

F32 = mybir.dt.float32
F32R = mybir.dt.float32r
ALU = mybir.AluOpType
ACT = mybir.ActivationFunctionType
AX = mybir.AxisListType.X

P = 128
D_MODEL = 1024
SEQ, DEC_SEQ, PAST = 256, 32, 512
T = SEQ + DEC_SEQ
D_INNER = 2048
HEADS_SSM, GROUPS, STATE = 32, 8, 128
HPG = HEADS_SSM // GROUPS
CONV_DIM = D_INNER + 2 * GROUPS * STATE
HEADS, NOPE, ROPE, VDIM = 16, 128, 64, 128
HALF = ROPE // 2
RANK = 512
D_FF = 4096
SCALE = (NOPE + ROPE) ** -0.5
ALPHA = 2 ** 0.25
RMS_EPS, LN_EPS = 1e-6, 1e-5
CHUNK = 64
KB = D_MODEL // P
RB = RANK // P
XB = D_INNER // P
CB = CONV_DIM // P
FB = D_FF // P
KEYS = PAST + DEC_SEQ
CW = 292
SC = 260
XW = 296

RING = 4
CK = 1024
LEAD = 3

N_XBC, A_XBC = 0, 0
N_SSD, A_SSD = N_XBC + CB, A_XBC + CB
N_QKV, A_QKV = N_SSD + 4 * GROUPS, A_SSD + 4 * GROUPS
N_SSM, A_SSM = N_QKV + 2 * RB, A_QKV + 2 * RB
N_ATT, A_ATT = N_SSM + 2 * KB, A_SSM + KB
ATT_CHUNKS, ATT_TURNS = 8, 12
ROUNDS = HEADS // 4
N_MLA, A_MLA = N_ATT + ATT_CHUNKS * ROUNDS, A_ATT + ATT_TURNS * ROUNDS
N_OUT, A_OUT = N_MLA + 2 * KB, A_MLA + KB
N_UP, A_UP = N_OUT + KB, A_OUT + KB
N_DOWN, A_DOWN = N_UP + FB, A_UP + FB
N_ALL = N_DOWN + 4 * KB
F_SSD, F_QKV = A_SSD, A_QKV
F_ATT = A_SSM
F_UP = F_ATT + ATT_TURNS * ROUNDS
G_SSM, G_MLA, G_OUT, G_DOWN = 0, KB, 2 * KB, 3 * KB

V_CONVW = 0
V_CONVB = V_CONVW + 4 * CB
V_GATE = V_CONVB + CB
V_SSMG = V_GATE + 2 * KB
V_QG = V_SSMG + XB
V_KVG = V_QG + RB
V_LN1G = V_KVG + RB
V_LN1B = V_LN1G + KB
V_LN2G = V_LN1B + KB
V_LN2B = V_LN2G + KB
V_D = V_LN2B + KB
V_DTB = V_D + XB
V_ALOG = V_DTB + 1
V_EPS = V_ALOG + 1
V_LNEPS = V_EPS + 1
V_ALL = V_LNEPS + 1
C_ID, C_ONE, C_TRI, C_MASK, C_COS, C_SIN, C_ALL = 0, 128, 416, 544, 928, 1216, 1504


def blk(t, i):
    return t[:, bass.ds(i, 1), :].rearrange("p a b -> p (a b)")


def layer_program(nc, wst, xT, misc, vecs, consts, ukT, cacheT, cacheK, kpeT, stateS, stateC,
                  o_y, o_ckv, o_kpe, o_ssm, o_conv):
    ctx = ExitStack()
    with ctx:
        base = (nc.sbuf_base + 31) // 32 * 32
        end = [0]

        def at(name, shape, off, dt=F32):
            n = 4
            for s in shape[1:]:
                n *= s
            assert base + off + n <= nc.sbuf_usable_end, (name, off, n)
            end[0] = off + n
            return nc.alloc_sbuf_tensor_at(name, shape, dt, offset=base + off)

        def after(name, shape, dt=F32):
            return at(name, shape, (end[0] + 31) // 32 * 32, dt)

        wraw = at("wraw", [P, RING, CK], 0)
        whi = after("whi", [P, RING, CK], F32R)
        wlo = after("wlo", [P, RING, CK], F32R)
        side = after("side", [P, 2, RANK])
        vec = after("vec", [P, V_ALL])
        con = after("con", [P, C_ALL])
        ones_r = after("ones_r", [HEADS_SSM, P], F32R)
        kpr = after("kpr", [P, T])
        kpall = after("kpall", [P, KEYS])
        gates = after("gates", [P, 2 * KB, T])
        Z = (end[0] + 31) // 32 * 32
        xh = at("xh", [P, KB, T], Z, F32R)
        xl = after("xl", [P, KB, T], F32R)
        xc = after("xc", [P, CB + 1, CW])
        Z3 = (end[0] + 31) // 32 * 32
        var_s = at("var_s", [P, GROUPS, T], Z3)
        Z4 = end[0]
        acum_h = at("acum_h", [HEADS_SSM, T], Z4, F32R)
        acum_l = after("acum_l", [HEADS_SSM, T], F32R)
        tokv = after("tokv", [P, 3, 3, HEADS_SSM])
        dec_b = after("dec_b", [P, HEADS_SSM])
        cstate = after("cstate", [P, CB, 3])
        cnew = after("cnew", [P, CB, 6])
        Z5 = (end[0] + 31) // 32 * 32
        x0 = at("x0", [P, KB, T], Z5)
        wmisc = after("wmisc", [P, KB, 96])
        xp = after("xp", [P, 2, XW])
        cv = after("cv", [P, 2, CW])
        dt_r = at("dt_r", [HEADS_SSM, T], Z5 + 22528)
        dt_a = after("dt_a", [HEADS_SSM, T])
        dt_v = after("dt_v", [HEADS_SSM, T])
        dta = after("dta", [HEADS_SSM, T])
        acum = after("acum", [HEADS_SSM, T])
        wend = after("wend", [HEADS_SSM, T])
        small = after("small", [HEADS_SSM, 8])
        dend = after("dend", [HEADS_SSM, HEADS_SSM])
        kt = after("kt", [HALF, 4, T])
        krot = after("krot", [HALF, 2, T])
        xcg = at("xcg", [P, 2, 4, CW], Z5)
        seg = after("seg", [P, 3, HPG, P])
        segs = after("segs", [DEC_SEQ, HPG, DEC_SEQ])
        xdt = after("xdt", [P, 3, 2 * P])
        wx = after("wx", [P, 3, 2 * P])
        btok = after("btok", [P, 3, STATE])
        rows_h = after("rows_h", [HEADS_SSM, HPG, T], F32R)
        rows_l = after("rows_l", [HEADS_SSM, HPG, T], F32R)
        s_in = after("s_in", [P, 2, 2 * P])
        s_dec = after("s_dec", [P, 2 * P])
        s_out = after("s_out", [P, 2, 2, 2 * P])
        e_row = after("e_row", [P, HPG, DEC_SEQ])
        c_dec = after("c_dec", [P, HPG, DEC_SEQ])
        zt = after("zt", [P, 2, T])
        ysb = after("ysb", [P, 2, T])
        sqs = after("sqs", [P, 2, T])
        yn_h = at("yn_h", [P, XB, T], Z4, F32R)
        yn_l = after("yn_l", [P, XB, T], F32R)
        qk = after("qk", [P, 2 * RB, T])
        qksq = after("qksq", [P, 2 * RB, T])
        yt = after("yt", [P, 2, T])
        q_h = at("q_h", [P, RB, T], Z, F32R)
        q_l = after("q_l", [P, RB, T], F32R)
        ckv_h = after("ckv_h", [P, RB, T], F32R)
        ckv_l = after("ckv_l", [P, RB, T], F32R)
        ssmg = after("ssmg", [P, KB, T])
        ckvn = after("ckvn", [P, RB, T])
        qn = after("qn", [P, RB, T])
        ckvT = after("ckvT", [P, RB, KEYS])
        ckvK = after("ckvK", [P, 5, RANK])
        Z6 = (end[0] + 31) // 32 * 32
        rqk = at("rqk", [P, 2, T], Z3)
        sig = after("sig", [P, 2, T])
        o_h = at("o_h", [P, HEADS, T], Z4, F32R)
        o_l = after("o_l", [P, HEADS, T], F32R)
        qab = after("qab", [P, 2, T])
        pe2 = after("pe2", [P, 2, T])
        kh = after("kh", [P, 4, SEQ])
        Z8 = (end[0] + 31) // 32 * 32
        of = at("of", [P, 4, T], Z8)
        rope_t = at("rope_t", [P, 4, T], Z8 + 4 * 384 * 4)
        prob = at("prob", [P, 4, 384], Z8)
        probT = after("probT", [P, 4, 384])
        Z7 = end[0]
        qn4 = at("qn4", [P, 4, T], Z + 4 * 4608 + 9216 + 4608)
        vh = at("vh", [P, 2, 4, VDIM], Z3)
        qlat = after("qlat", [P, RB, P])
        olat_l = at("olat_l", [P, RB, P], end[0] - RB * P * 4, F32R)
        ssc = after("ssc", [P, KEYS])
        qz = after("qz", [P, 4, DEC_SEQ])
        assert end[0] <= Z4, (end[0], Z4)
        stat = at("stat", [P, 6, 12], Z7)
        ssT = after("ssT", [P, 5, P])
        olat_h = after("olat_h", [P, RB, P], F32R)
        mix_h = at("mix_h", [P, KB, T], Z, F32R)
        mix_l = after("mix_l", [P, KB, T], F32R)
        xr = at("xr", [P, KB, T], Z + 4 * 4608 + 9216)
        hp = after("hp", [P, KB, T])
        hsq = after("hsq", [P, KB, T])
        mean = at("mean", [P, 3, T], Z3 + 4 * T * 4)
        mixt = at("mixt", [P, 2, T], Z3)
        h_h = at("h_h", [P, KB, T], Z, F32R)
        h_l = after("h_l", [P, KB, T], F32R)
        h = at("h", [P, KB, T], Z + 4 * 4608)
        rl = at("rl", [P, 2, T], Z + 4 * 4608 + 9216)
        ff = after("ff", [P, 2, T])
        yp = at("yp", [P, KB, T], Z + 4 * 4608 + 9216)
        ysq = after("ysq", [P, KB, T])
        lnm = after("lnm", [P, 3, T])
        ff_h = after("ff_h", [P, FB, T], F32R)
        ff_l = after("ff_l", [P, FB, T], F32R)

        def psum(name, shape):
            return ctx.enter_context(nc.psum_tensor(name, shape, F32))

        ps_acc = psum("ps_acc", [P, 2, 512])
        ps_row = psum("ps_row", [P, 2, 512])
        ps_cb = psum("ps_cb", [P, 512])
        ps_tr = psum("ps_tr", [P, 512])
        ps_s = psum("ps_s", [P, 512])
        ps_ss = psum("ps_ss", [P, 512])
        ps_att = [ps_row[:, 0, :], ps_row[:, 1, :], ps_cb[:, :], ps_tr[:, :]]

        ident = con[:, C_ID:C_ID + P]
        ones = con[:, C_ONE:C_ONE + P]
        one_row = con[0:HEADS_SSM, C_ONE:C_ONE + T]
        tri = con[:, C_TRI:C_TRI + P]
        mask = con[:, C_MASK:C_MASK + 384]
        cos = con[:, C_COS:C_COS + T]
        sin = con[:, C_SIN:C_SIN + T]

        def v1(c, n=1):
            return vec[:, c:c + n]

        def vd(c):
            return vec[:, bass.ds(c, 1)]

        def sem(name):
            return ctx.enter_context(nc.semaphore(name))

        def sems(*names):
            return [sem(n) for n in names]

        in_loaded, late_loaded, x_in0, x_in1, split_hi = sems(
            "in_loaded", "late_loaded", "x_in0", "x_in1", "split_hi")
        split_lo, chunk_used, freed_act, freed_dve, x_split = sems(
            "split_lo", "chunk_used", "freed_act", "freed_dve", "x_split")
        misc_done, xp_state, xp_ready, xp_saved, tap3_done = sems(
            "misc_done", "xp_state", "xp_ready", "xp_saved", "tap3_done")
        tap_chain, conv_done, silu_done, stored, dt_pre = sems(
            "tap_chain", "conv_done", "silu_done", "stored", "dt_pre")
        m_dve, m_act, acum_ready, dend_ready, m_pe = sems(
            "m_dve", "m_act", "acum_ready", "dend_ready", "m_pe")
        mid_done, krot_done, staged, rows_made, rows_done = sems(
            "mid_done", "krot_done", "staged", "rows_made", "rows_done")
        tr_done, tr_free, cb_done, seg_done, exp_done = sems(
            "tr_done", "tr_free", "cb_done", "seg_done", "exp_done")
        m_done, c_done, d3, y_done, yz_done = sems(
            "m_done", "c_done", "d3", "y_done", "yz_done")
        y_free, s_done, s_ready, wx_done, sq_done = sems(
            "y_free", "s_done", "s_ready", "wx_done", "sq_done")
        ss_done, ss_free, std_done, rstd_done, norm_t = sems(
            "ss_done", "ss_free", "std_done", "rstd_done", "norm_t")
        norm_h, norm_done, lat_sq, lat_sum, lat_std = sems(
            "norm_h", "norm_done", "lat_sq", "lat_sum", "lat_std")
        lat_done, lat_dve, tok_pe, tok_cp, ckv_out = sems(
            "lat_done", "lat_dve", "tok_pe", "tok_cp", "ckv_out")
        sig_done, qlat_done, qlat_cp, half_ready, v_ready = sems(
            "sig_done", "qlat_done", "qlat_cp", "half_ready", "v_ready")
        pe_done, sc_done, sc_evac, amax, samax = sems(
            "pe_done", "sc_done", "sc_evac", "amax", "samax")
        aexp, saexp, anorm, at_done, at_cp = sems(
            "aexp", "saexp", "anorm", "at_done", "at_cp")
        ssc_done, ssc_rec, st_done, st_cp, ol_done = sems(
            "ssc_done", "ssc_rec", "st_done", "st_cp", "ol_done")
        ol_hi, ol_lo, o_done, o_evac, o_hi = sems(
            "ol_hi", "ol_lo", "o_done", "o_evac", "o_hi")
        o_lo, d5, mix_g, mix_t, mix_hi = sems(
            "o_lo", "d5", "mix_g", "mix_t", "mix_hi")
        mix_lo, xr_loaded, ln_dve, ln_act, ln_pe = sems(
            "mix_lo", "xr_loaded", "ln_dve", "ln_act", "ln_pe")
        ff_sq, ff_hi, ff_lo, ln_sum = sems(
            "ff_sq", "ff_hi", "ff_lo", "ln_sum")
        conv_out = sem("conv_out")
        raw_loaded = [sem(f"raw_loaded{i}") for i in range(RING)]
        state_in = [sem(f"state_in{i}") for i in range(2)]
        s_stored = [sem(f"s_stored{i}") for i in range(2)]
        side_in = [sem(f"side_in{i}") for i in range(2)]

        block = ctx.enter_context(nc.Block())

        @block.sync
        def _(sp):
            sp.dma_start(x0[:, 0:4, :], xT[:, 0:4, :]).then_inc(x_in0, 16)
            sp.dma_start(x0[:, 4:8, :], xT[:, 4:8, :]).then_inc(x_in1, 16)
            for s in range(RING):
                sp.dma_start(wraw[:, s, :], wst[s]).then_inc(raw_loaded[s], 16)
                if s == 0:
                    for tile, src in ((wmisc, misc), (vec, vecs), (con, consts), (cstate, stateC)):
                        sp.dma_start(tile[:], src).then_inc(in_loaded, 16)
            with sp.Fori(1, N_ALL // RING) as i:
                for s in range(RING):
                    sp.wait_ge(split_lo, RING * i + s - 3)
                    sp.dma_start(wraw[:, s, :], wst[bass.ds(RING * i + s, 1)].rearrange("a p c -> (a p) c")
                                 ).then_inc(raw_loaded[s], 16)
            for q in range(2):
                sp.wait_ge(ln_dve, 17 + q)
                sp.dma_start(o_y[:, 4 * q:4 * q + 4, :], yp[:, 4 * q:4 * q + 4, :]).then_inc(stored, 16)
            sp.wait_ge(stored, 16 * 3)
            sp.wait_ge(conv_out, 16)
            sp.wait_ge(ckv_out, 16)
            for s in s_stored:
                sp.wait_ge(s, 16 * GROUPS + 1)

        @block.tensor
        def _(pe):
            def passes(out, w, wl, mh, ml, first, last):
                pe.matmul(out, w, mh, start=first, stop=False)
                pe.matmul(out, w, ml, start=False, stop=False)
                return pe.matmul(out, wl, mh, start=False, stop=last)

            def chunk(out, n, slot, mh, ml, k0=0, first=True, last=True):
                pe.wait_ge(split_lo, n + 1)
                for k in range(8):
                    c = slice(k * P, (k + 1) * P)
                    mm = passes(out, whi[:, slot, c], wlo[:, slot, c], mh[:, k0 + k, :], ml[:, k0 + k, :],
                                first and k == 0, last and k == 7)
                return mm

            pe.sem_inc(freed_act, 2)
            pe.sem_inc(freed_dve, 2)
            pe.sem_inc(chunk_used, 1)
            for s in (tr_free, m_done, y_free, s_ready, ss_free, rows_done, *s_stored):
                pe.sem_inc(s, 1)
            pe.sem_inc(norm_done, 1)
            for s in (yz_done, xp_saved, qlat_done):
                pe.sem_inc(s, 2)

            pe.wait_ge(x_in0, 16)
            pe.wait_ge(x_in1, 16)
            pe.wait_ge(in_loaded, 64)
            for k in range(KB):
                mm = pe.matmul(ps_ss[0:96, 0:T], wmisc[:, k, :], x0[:, k, :], start=k == 0, stop=k == KB - 1)
            mm.then_inc(misc_done, 1)
            pe.wait_ge(x_split, 4)

            with pe.Fori(0, CB // 4) as i:
                for k in range(4):
                    b = 4 * i + k
                    pe.wait_ge(freed_act, b + 1)
                    chunk(ps_acc[:, k % 2, 0:T], N_XBC + b, k, xh, xl).then_inc(chunk_used, 1)

            pe.wait_ge(m_act, 6)
            pe.wait_ge(dend_ready, 1)
            for t, (c0, n) in enumerate(((0, P), (P, P), (SEQ, DEC_SEQ))):
                for j, src in enumerate((dt_v, acum, wend)):
                    mm = pe.transpose(ps_tr[0:n, (3 * t + j) * 32:(3 * t + j + 1) * 32], src[:, c0:c0 + n],
                                      ident[0:32, 0:32])
            mm = pe.matmul(ps_cb[:, 0:HEADS_SSM], one_row[:, 0:P], dend[:], start=True, stop=True)
            mm.then_inc(m_pe, 1)

            def decay_rows(g):
                pe.wait_ge(rows_made, 2 * g + 2)
                pe.wait_ge(y_free, g + 1)
                for r in range(2):
                    out = ps_row[:, r, :].rearrange("p (h i) -> p h i", h=2)
                    pe.matmul(out, ones_r[:], rows_h[:, 2 * r:2 * r + 2, 0:SEQ], start=True, stop=False)
                    pe.matmul(out, ones_r[:], rows_l[:, 2 * r:2 * r + 2, 0:SEQ], start=False, stop=True)
                rs = ps_ss[:, 384:512].rearrange("p (h i) -> p h i", h=HPG)
                pe.matmul(rs, ones_r[:], rows_h[:, :, SEQ:T], start=True, stop=False)
                pe.matmul(rs, ones_r[:], rows_l[:, :, SEQ:T], start=False, stop=True).then_inc(rows_done, 1)

            decay_rows(0)
            with pe.Fori(0, GROUPS // 2) as i:
                for p in range(2):
                    g = 2 * i + p

                    def trans(t):
                        c0, n = ((0, P), (P, P), (SC, DEC_SEQ))[t]
                        pe.wait_ge(tr_free, 3 * g + t + 1)
                        for j in range(3):
                            mm = pe.transpose(ps_tr[0:n, j * P:(j + 1) * P], xcg[:, p, j, c0:c0 + n], ident)
                        mm.then_inc(tr_done, 1)

                    def gemm(k):
                        pe.wait_ge(freed_act, F_SSD + 4 * g + k + 1)
                        chunk(ps_acc[:, k % 2, 0:T], N_SSD + 4 * g + k, k, xh, xl).then_inc(chunk_used, 1)

                    pe.wait_ge(staged, 3 * g + 3)
                    trans(0)
                    pe.wait_ge(m_done, g + 1)
                    pe.matmul(ps_cb[:, 0:SEQ], xcg[:, p, 2, 0:P], xcg[:, p, 3, 0:SEQ], start=True, stop=True)
                    pe.matmul(ps_cb[:, SEQ:384], xcg[:, p, 2, P:SEQ], xcg[:, p, 3, P:SEQ], start=True, stop=True)
                    pe.matmul(ps_cb[0:DEC_SEQ, 384:384 + DEC_SEQ], xcg[:, p, 2, SC:CW], xcg[:, p, 3, SC:CW],
                              start=True, stop=True).then_inc(cb_done, 1)
                    gemm(0)
                    trans(1)
                    gemm(1)
                    trans(2)
                    gemm(2)
                    pe.wait_ge(m_done, g + 2)
                    pe.wait_ge(c_done, g + 1)
                    pe.wait_ge(state_in[p], 16 * (i + 1))
                    pe.wait_ge(wx_done, 3 * g + 3)
                    for h4 in range(HPG):
                        r, o = h4 // 2, 64 * (h4 % 2)
                        hc = slice(64 * h4, 64 * h4 + 64)
                        y = ps_row[o:o + 64, r, :]
                        pe.matmul(y[:, 0:SEQ].rearrange("p (a b) -> p a b", a=2), xdt[:, 0, hc], seg[:, 0:2, h4, :],
                                  start=True, stop=False)
                        pe.matmul(y[:, P:SEQ], xdt[:, 1, hc], seg[:, 2, h4, :], start=False, stop=True)
                        pe.matmul(y[:, SEQ:T], xdt[0:DEC_SEQ, 2, hc], segs[:, h4, :], start=True, stop=False)
                        mm = pe.matmul(y[:, SEQ:T], s_in[:, p, hc], c_dec[:, h4, :], start=False, stop=True)
                    mm.then_inc(y_done, 1)
                    pe.wait_ge(s_ready, g + 1)
                    pe.matmul(ps_s[:, 0:2 * P], btok[:, 0, :], wx[:, 0, :], start=True, stop=False)
                    pe.matmul(ps_s[:, 0:2 * P], btok[:, 1, :], wx[:, 1, :], start=False, stop=True)
                    pe.matmul(ps_s[:, 2 * P:4 * P], btok[0:DEC_SEQ, 2, :], wx[0:DEC_SEQ, 2, :],
                              start=True, stop=True).then_inc(s_done, 1)
                    gemm(3)
                    decay_rows(g + 1)
                    pe.wait_ge(ss_free, g + 1)
                    pe.wait_ge(sq_done, g + 1)
                    pe.matmul(ps_ss[:, 0:T], ones, sqs[:, 0, :], start=True, stop=False)
                    pe.matmul(ps_ss[:, 0:T], ones, sqs[:, 1, :], start=False, stop=True).then_inc(ss_done, 1)

            with pe.Fori(0, 2) as i:
                for k in range(4):
                    b = 4 * i + k
                    pe.wait_ge(freed_act, F_QKV + b + 1)
                    chunk(ps_acc[:, k % 2, 0:T], N_QKV + b, k, xh, xl).then_inc(chunk_used, 1)

            pe.wait_ge(lat_sq, 1)
            for j in range(2):
                for k in range(RB):
                    mm = pe.matmul((ps_ss if j else ps_s)[:, 0:T], ones, qksq[:, RB * j + k, :],
                                   start=k == 0, stop=k == RB - 1)
            mm.then_inc(lat_sum, 1)
            pe.wait_ge(norm_done, GROUPS + 1)
            pe.wait_ge(freed_act, F_ATT + 2)
            with pe.Fori(0, KB // 2) as i:
                for k in range(4):
                    if k % 2 == 0:
                        pe.wait_ge(freed_dve, G_SSM + 2 * i + k // 2 + 1)
                    mm = chunk(ps_acc[:, k // 2, 0:T], N_SSM + 4 * i + k, k, yn_h, yn_l, 8 * (k % 2),
                               k % 2 == 0, k % 2 == 1)
                    mm.then_inc(chunk_used, 1)

            pe.wait_ge(lat_dve, 2)
            for k in range(RB):
                mm = pe.transpose(ps_tr[0:DEC_SEQ, k * P:(k + 1) * P], ckvn[:, k, SEQ:T], ident)
            mm.then_inc(tok_pe, 1)
            pe.wait_ge(freed_dve, G_MLA + 2)
            pe.wait_ge(lat_dve, 4)
            pe.wait_ge(tok_cp, 2)
            pe.wait_ge(late_loaded, 16 * 4)
            with pe.Fori(0, ROUNDS) as i:
                n0 = N_ATT + ATT_CHUNKS * i
                f0 = F_ATT + ATT_TURNS * i

                def turn(j):
                    pe.wait_ge(freed_act, f0 + j + 1)
                    return ps_acc[:, j % 2, :]

                for c in range(3):
                    pe.wait_ge(split_lo, n0 + c + 1)
                    for j in range(2):
                        acc = turn(2 * c + j)
                        for k in range(RB):
                            w = slice((RB * j + k) * P, (RB * j + k + 1) * P)
                            mm = passes(acc[:, 0:T], whi[:, c, w], wlo[:, c, w], q_h[:, k, :], q_l[:, k, :],
                                        k == 0, k == RB - 1)
                        mm.then_inc(chunk_used if j else half_ready, 1)
                for c in range(3, 5):
                    s = c % RING
                    pe.wait_ge(split_lo, n0 + c + 1)
                    for j in range(2):
                        acc = turn(2 * c + j)
                        for k in range(RB):
                            w = slice((RB * j + k) * P, (RB * j + k + 1) * P)
                            mm = passes(acc[:, 0:SEQ], whi[:, s, w], wlo[:, s, w], ckv_h[:, k, 0:SEQ],
                                        ckv_l[:, k, 0:SEQ], k == 0, k == RB - 1)
                        mm.then_inc(chunk_used if j else half_ready, 1)
                pe.wait_ge(freed_act, f0 + 4 + 2)
                for h4 in range(4):
                    pe.wait_ge(side_in[h4 % 2], 16 * (2 * i + h4 // 2 + 1))
                    for c in range(RB):
                        mm = pe.matmul(ps_s[:, c * P + 32 * h4:c * P + 32 * h4 + 32],
                                       side[:, h4 % 2, c * P:(c + 1) * P], qn4[:, h4, SEQ:T],
                                       start=True, stop=True)
                    mm.then_inc(qlat_done, 1)
                pe.wait_ge(pe_done, i + 1)
                pe.wait_ge(freed_act, f0 + 10 + 2)
                for h4 in range(4):
                    pr, o = h4 // 2, 64 * (h4 % 2)
                    s = ps_att[h4]
                    for q0, k1, c in ((0, P, 0), (P, SEQ, P)):
                        out = s[:, c:c + k1]
                        pe.matmul(out, qn4[:, h4, q0:q0 + P], kh[:, h4, 0:k1], start=True, stop=False)
                        mm = pe.matmul(out, pe2[o:o + 64, pr, q0:q0 + P], kpr[o:o + 64, 0:k1],
                                       start=False, stop=True)
                    mm.then_inc(sc_done, 1)
                pe.wait_ge(qlat_cp, i + 1)
                pe.wait_ge(split_lo, n0 + 6)
                for (k0, k1, bank) in ((0, PAST, ps_s), (PAST, KEYS, ps_ss)):
                    for c in range(RB):
                        pe.matmul(bank[:, 0:k1 - k0], qlat[:, c, :], ckvT[:, c, k0:k1], start=c == 0, stop=False)
                    mm = pe.matmul(bank[:, 0:k1 - k0], qz[:].rearrange("p h q -> p (h q)"), kpall[:, k0:k1],
                                   start=False, stop=True)
                    mm.then_inc(ssc_done if k0 else chunk_used, 1)
                for c in (6, 7):
                    s = c % RING
                    pe.wait_ge(split_lo, n0 + c + 1)
                    acc = turn(4 + c)
                    for t in range(2):
                        for k in range(RB):
                            w = slice(k * 2 * P, (k + 1) * 2 * P)
                            f = slice(t * P, (t + 1) * P)
                            out = acc[:, t * 2 * P:(t + 1) * 2 * P]
                            pe.matmul(out, ckv_h[:, k, f], whi[:, s, w], start=k == 0, stop=False)
                            pe.matmul(out, ckv_h[:, k, f], wlo[:, s, w], start=False, stop=False)
                            mm = pe.matmul(out, ckv_l[:, k, f], whi[:, s, w], start=False, stop=k == RB - 1)
                    mm.then_inc(v_ready, 1)
                pe.wait_ge(anorm, 2 * i + 1)
                for h4 in range(4):
                    for j in range(3):
                        mm = pe.transpose(ps_att[h4][:, j * P:(j + 1) * P], prob[:, h4, j * P:(j + 1) * P], ident)
                    mm.then_inc(at_done, 1)
                pe.wait_ge(anorm, 2 * i + 2)
                for j in range(5):
                    n = P if j < 4 else DEC_SEQ
                    mm = pe.transpose(ps_s[:, j * P:(j + 1) * P] if j < 4 else ps_ss[0:DEC_SEQ, 0:P],
                                      ssc[:, j * P:j * P + n], ident)
                mm.then_inc(st_done, 1)
                pe.wait_ge(st_cp, i + 1)
                for c in range(RB):
                    for j in range(5):
                        n = P if j < 4 else DEC_SEQ
                        mm = pe.matmul(ps_s[:, c * P:(c + 1) * P], ckvK[0:n, j, c * P:(c + 1) * P], ssT[0:n, j, :],
                                       start=j == 0, stop=j == 4)
                mm.then_inc(ol_done, 1)
                pe.wait_ge(freed_act, f0 + 12 + 2)
                for h4 in range(4):
                    pe.wait_ge(at_cp, 4 * i + h4 + 1)
                    o = ps_att[h4]
                    pe.matmul(o[:, 0:SEQ], vh[:, 0, h4, :], probT[:, h4, 0:SEQ], start=True, stop=False)
                    mm = pe.matmul(o[:, P:SEQ], vh[:, 1, h4, :], probT[:, h4, SEQ:384], start=False, stop=True)
                    mm.then_inc(o_done, 1)
                pe.wait_ge(ol_lo, i + 1)
                for h4 in range(4):
                    s = (6 + h4 // 2) % RING
                    for k in range(RB):
                        w = slice((2 * k + h4 % 2) * P, (2 * k + h4 % 2 + 1) * P)
                        q = slice(32 * h4, 32 * h4 + 32)
                        mm = passes(ps_ss[:, q], whi[:, s, w], wlo[:, s, w], olat_h[:, k, q], olat_l[:, k, q],
                                    k == 0, k == RB - 1)
                    if h4 % 2:
                        mm.then_inc(chunk_used, 1)

            pe.wait_ge(freed_act, F_UP + 2)
            pe.wait_ge(o_lo, ROUNDS)
            with pe.Fori(0, KB // 2) as i:
                for k in range(4):
                    if k % 2 == 0:
                        pe.wait_ge(freed_dve, G_MLA + 2 * i + k // 2 + 1)
                    mm = chunk(ps_acc[:, k // 2, 0:T], N_MLA + 4 * i + k, k, o_h, o_l, 8 * (k % 2),
                               k % 2 == 0, k % 2 == 1)
                    mm.then_inc(chunk_used, 1)

            pe.wait_ge(mix_lo, KB)
            pe.wait_ge(freed_dve, G_OUT + 2)
            with pe.Fori(0, 2) as i:
                for k in range(4):
                    pe.wait_ge(freed_dve, G_OUT + 4 * i + k + 1)
                    chunk(ps_acc[:, k % 2, 0:T], N_OUT + 4 * i + k, k, mix_h, mix_l).then_inc(chunk_used, 1)

            def norm_sums(run, sq, summed, ac):
                pe.wait_ge(ln_sum, summed)
                pe.matmul(ps_s[:, 0:T], ones, run, start=True, stop=True).then_inc(ln_pe, 1)
                for k in range(KB):
                    if k % 4 == 0:
                        pe.wait_ge(ln_act, ac + 1 + k // 4)
                    mm = pe.matmul(ps_ss[:, 0:T], ones, sq[:, k, :], start=k == 0, stop=k == KB - 1)
                mm.then_inc(ln_pe, 1)

            norm_sums(mean[:, 1, :], hsq, KB + 1, 0)
            pe.wait_ge(ln_dve, 10)
            with pe.Fori(0, FB // 4) as i:
                for k in range(4):
                    pe.wait_ge(freed_act, F_UP + 4 * i + k + 1)
                    chunk(ps_acc[:, k % 2, 0:T], N_UP + 4 * i + k, k, h_h, h_l).then_inc(chunk_used, 1)
            pe.wait_ge(ff_lo, FB)
            pe.wait_ge(freed_act, F_UP + FB + 2)

            def down(i, par):
                pe.wait_ge(freed_dve, G_DOWN + i + 1)
                for k in range(4):
                    mm = chunk(ps_acc[:, par, 0:T], N_DOWN + 4 * i + k, k, ff_h, ff_l, 8 * k, k == 0, k == 3)
                    mm.then_inc(chunk_used, 1)

            with pe.Fori(0, KB // 2) as i:
                down(2 * i, 0)
                down(2 * i + 1, 1)
            norm_sums(lnm[:, 1, :], ysq, 2 * KB + 2, 5)

        @block.scalar
        def _(act):
            def hi(n, slot):
                act.wait_ge(raw_loaded[slot], 16 * (n // RING + 1))
                act.copy(whi[:, slot, :], wraw[:, slot, :]).then_inc(split_hi, 1)

            def hi_step(n0, turn, k):
                m = k + LEAD
                act.wait_ge(raw_loaded[m % RING], 16 * (turn + m // RING + 1))
                act.wait_ge(chunk_used, n0 + m - 2)
                act.copy(whi[:, m % RING, :], wraw[:, m % RING, :]).then_inc(split_hi, 1)

            for n in range(LEAD):
                hi(n, n)

            act.wait_ge(in_loaded, 64)
            act.wait_ge(dt_pre, 1)
            act.activation(dt_a[:], dt_a[:], ACT.Exp).then_inc(m_act, 1)
            act.wait_ge(m_act, 1)
            act.activation(dt_a[:], dt_a[:], ACT.Ln, bias=1.0).then_inc(m_act, 1)
            act.activation(small[:, 0:1], vec[0:HEADS_SSM, V_ALOG:V_ALOG + 1], ACT.Exp).then_inc(m_act, 1)
            act.wait_ge(acum_ready, 2)
            act.activation(wend[:, 0:SEQ], acum[:, 0:SEQ], ACT.Exp, bias=acum[:, SEQ - 1:SEQ],
                           scale=-1.0).then_inc(m_act, 1)
            act.activation(wend[:, SEQ:T], acum[:, SEQ:T], ACT.Exp, bias=acum[:, T - 1:T],
                           scale=-1.0).then_inc(m_act, 1)
            act.activation(small[:, 1:2], acum[:, T - 1:T], ACT.Exp).then_inc(m_act, 1)
            act.wait_ge(krot_done, 2)
            act.dma_start(o_kpe, krot[:]).then_inc(stored, 16)

            act.wait_ge(in_loaded, 64)
            with act.Fori(0, CB // 4) as i:
                for k in range(4):
                    b, u = 4 * i + k, k % 2
                    hi_step(4 * i, i, k)
                    act.wait_ge(chunk_used, N_XBC + b + 2)
                    act.wait_ge(xp_saved, b + 1)
                    act.copy(xp[:, u, 264:XW], ps_acc[:, u, SEQ:T])
                    act.copy(xp[:, u, 4:260], ps_acc[:, u, 0:SEQ]).then_inc(freed_act, 1)
                    act.wait_ge(freed_act, b + 3)
                    act.wait_ge(xp_state, b + 1)
                    act.activation(cv[:, u, :], xp[:, u, 4:XW], ACT.Identity, bias=vd(V_CONVB + b),
                                   scale=vd(V_CONVW + 3 * CB + b)).then_inc(tap3_done, 1)
                    act.wait_ge(conv_done, b + 2)
                    act.activation(blk(xc, b), cv[:, 1 - u, :], ACT.Silu).then_inc(silu_done, 1)
            act.wait_ge(conv_done, CB + 2)
            act.activation(xc[:, CB, :], cv[:, 1, :], ACT.Silu).then_inc(silu_done, 1)

            with act.Fori(0, GROUPS // 2) as i:
                for p in range(2):
                    g = 2 * i + p
                    n0 = N_SSD + 4 * g

                    def z_block(k):
                        act.wait_ge(chunk_used, n0 + k + 2)
                        act.activation(zt[:, k, :], ps_acc[:, k, 0:T], ACT.Silu).then_inc(freed_act, 1)

                    def gate_block(k):
                        act.wait_ge(chunk_used, n0 + k + 2)
                        act.activation(blk(gates, 2 * g + k - 2), ps_acc[:, k % 2, 0:T], ACT.Identity,
                                       bias=vd(V_GATE + 2 * g + k - 2)).then_inc(freed_act, 1)

                    hi_step(n0, N_SSD // RING + g, 0)
                    z_block(0)
                    act.wait_ge(seg_done, g + 1)
                    act.activation(seg[:], seg[:], ACT.Exp)
                    act.activation(segs[:], segs[:], ACT.Exp)
                    act.activation(e_row[:], ps_ss[:, 384:512].rearrange("p (h i) -> p h i", h=HPG),
                                   ACT.Exp).then_inc(exp_done, 1)
                    hi_step(n0, N_SSD // RING + g, 1)
                    hi_step(n0, N_SSD // RING + g, 2)
                    z_block(1)
                    hi_step(n0, N_SSD // RING + g, 3)
                    gate_block(2)
                    act.wait_ge(yz_done, g + 3)
                    act.activation(sqs[:], xc[:, bass.ds(2 * g + 1, 2), 0:T], ACT.Square).then_inc(sq_done, 1)
                    gate_block(3)
                    act.wait_ge(ss_done, g + 1)
                    act.copy(blk(var_s, g), ps_ss[:, 0:T]).then_inc(ss_free, 1)
                    act.wait_ge(s_ready, g + 2)
                    for q in range(2):
                        act.dma_start(o_ssm[q, bass.ds(g, 1)].rearrange("a p c -> (a p) c"),
                                      s_out[:, p, q, :]).then_inc(s_stored[p], 16)

            with act.Fori(0, 2) as i:
                for k in range(4):
                    j = 4 * i + k
                    hi_step(N_QKV + 4 * i, N_QKV // RING + i, k)
                    act.wait_ge(ss_free, GROUPS + 1)
                    act.activation(blk(var_s, j), blk(var_s, j), ACT.Sqrt, scale=1.0 / (2 * P),
                                   bias=v1(V_EPS)).then_inc(std_done, 1)
                    for s in s_stored:
                        act.wait_ge(s, 16 * GROUPS + 1)
                    act.wait_ge(chunk_used, N_QKV + j + 2)
                    act.copy(blk(qk, j), ps_acc[:, k % 2, 0:T]).then_inc(freed_act, 1)
                    act.wait_ge(norm_t, j + 1)
                    act.copy(yn_h[:, bass.ds(2 * j, 2), :], yt[:]).then_inc(norm_h, 1)

            act.wait_ge(freed_act, F_ATT + 2)
            act.activation(qksq[:], qk[:], ACT.Square).then_inc(lat_sq, 1)
            act.wait_ge(lat_sum, 1)
            act.activation(rqk[:, 0, :], ps_s[:, 0:T], ACT.Sqrt, scale=1.0 / RANK, bias=v1(V_EPS)).then_inc(lat_std, 1)
            act.activation(rqk[:, 1, :], ps_ss[:, 0:T], ACT.Sqrt, scale=1.0 / RANK, bias=v1(V_EPS)).then_inc(lat_std, 1)
            act.wait_ge(lat_dve, 2)
            act.copy(q_h[:], qn[:]).then_inc(lat_done, 1)
            act.copy(ckv_h[:], ckvn[:]).then_inc(lat_done, 1)
            act.dma_start(o_ckv, ckvn[:]).then_inc(ckv_out, 16)

            def gate_phase(n0, gate0, freed0):
                with act.Fori(0, KB // 2) as i:
                    for j in range(2):
                        hi_step(n0 + 4 * i, n0 // RING + i, 2 * j)
                        act.wait_ge(freed_dve, freed0 + 2 * i + j + 1)
                        act.activation(sig[:, j, :], blk(gates, gate0 + 2 * i + j), ACT.Sigmoid).then_inc(sig_done, 1)
                        hi_step(n0 + 4 * i, n0 // RING + i, 2 * j + 1)
                        if gate0:
                            act.wait_ge(mix_t, 2 * i + j + 1)
                            act.copy(blk(mix_h, 2 * i + j), mixt[:, j, :]).then_inc(mix_hi, 1)

            gate_phase(N_SSM, 0, G_SSM)
            act.wait_ge(ckv_out, 16)

            with act.Fori(0, ROUNDS) as i:
                n0, turn = N_ATT + ATT_CHUNKS * i, N_ATT // RING + 2 * i
                for c in range(5):
                    hi_step(n0, turn, c)
                    for j in range(2):
                        if j:
                            act.wait_ge(chunk_used, n0 + c + 2)
                        else:
                            act.wait_ge(half_ready, 5 * i + c + 1)
                        if c < 2:
                            act.copy(qn4[:, 2 * c + j, :], ps_acc[:, j, 0:T]).then_inc(freed_act, 1)
                        elif c == 2:
                            act.copy(qab[:, j, :], ps_acc[:, j, 0:T]).then_inc(freed_act, 1)
                        else:
                            act.copy(kh[:, 2 * (c - 3) + j, :], ps_acc[:, j, 0:SEQ]).then_inc(freed_act, 1)
                hi_step(n0, turn, 5)
                act.wait_ge(amax, i + 1)
                for h4 in range(4):
                    for q, (a, b) in enumerate(((0, P), (P, 384))):
                        e = act.activation(prob[:, h4, a:b], prob[:, h4, a:b], ACT.Exp,
                                           bias=stat[:, 1, 4 * q + h4:4 * q + h4 + 1],
                                           accum_out=stat[:, 2, 4 * q + h4:4 * q + h4 + 1])
                e.then_inc(aexp, 1)
                act.wait_ge(samax, i + 1)
                act.activation(ssc[:], ssc[:], ACT.Exp, bias=stat[:, 1, 8:9],
                               accum_out=stat[:, 2, 8:9]).then_inc(saexp, 1)
                hi_step(n0, turn, 6)
                for j in range(2):
                    act.wait_ge(v_ready, 2 * i + j + 1)
                    act.copy(vh[:, :, 2 * j:2 * j + 2, :].rearrange("p t h v -> p t (h v)"),
                             ps_acc[:, j, :].rearrange("p (t c) -> p t c", t=2)).then_inc(freed_act, 1)
                for h4 in range(4):
                    act.wait_ge(at_done, 4 * i + h4 + 1)
                    act.copy(probT[:, h4, :], ps_att[h4][:, 0:384]).then_inc(at_cp, 1)
                act.wait_ge(ol_done, i + 1)
                act.copy(olat_h[:].rearrange("p c q -> p (c q)"), ps_s[:]).then_inc(ol_hi, 1)
                for h4 in range(4):
                    act.wait_ge(o_done, 4 * i + h4 + 1)
                    act.copy(of[:, h4, 0:SEQ], ps_att[h4][:, 0:SEQ])
                act.wait_ge(chunk_used, n0 + 9)
                act.copy(of[:, :, SEQ:T], ps_ss[:, 0:P].rearrange("p (h q) -> p h q", h=4)).then_inc(o_evac, 1)
                act.wait_ge(o_evac, i + 1)
                act.copy(o_h[:, bass.ds(4 * i, 4), :], of[:]).then_inc(o_hi, 1)
                hi_step(n0, turn, 7)

            gate_phase(N_MLA, KB, G_MLA)

            def only_split(n0, rounds):
                with act.Fori(0, rounds) as i:
                    for k in range(4):
                        hi_step(n0 + 4 * i, n0 // RING + i, k)

            only_split(N_OUT, 2)
            for q in range(2):
                act.wait_ge(ln_dve, 2 + q)
                act.activation(hsq[:, 4 * q:4 * q + 4, :], hp[:, 4 * q:4 * q + 4, :], ACT.Square).then_inc(ln_act, 1)
            act.wait_ge(ln_pe, 2)
            act.activation(mean[:, 1, :], ps_ss[:, 0:T], ACT.Sqrt, scale=1.0 / D_MODEL, bias=v1(V_LNEPS)).then_inc(ln_act, 1)
            for q in range(2):
                act.wait_ge(ln_dve, 7 + q)
                act.copy(h_h[:, 4 * q:4 * q + 4, :], h[:, 4 * q:4 * q + 4, :]).then_inc(ln_act, 1)

            with act.Fori(0, FB // 4) as i:
                for k in range(4):
                    b, u = 4 * i + k, k % 2
                    hi_step(N_UP + 4 * i, N_UP // RING + i, k)
                    act.wait_ge(chunk_used, N_UP + b + 2)
                    act.activation(rl[:, u, :], ps_acc[:, u, 0:T], ACT.Relu).then_inc(freed_act, 1)
                    act.wait_ge(ff_sq, b + 1)
                    act.copy(blk(ff_h, b), ff[:, u, :]).then_inc(ff_hi, 1)

            only_split(N_DOWN, KB - 1)
            hi_step(N_ALL - 4, N_ALL // RING - 1, 0)
            for q in range(2):
                act.wait_ge(ln_dve, 12 + q)
                act.activation(ysq[:, 4 * q:4 * q + 4, :], yp[:, 4 * q:4 * q + 4, :], ACT.Square).then_inc(ln_act, 1)
            act.wait_ge(ln_pe, 4)
            act.activation(lnm[:, 1, :], ps_ss[:, 0:T], ACT.Sqrt, scale=1.0 / D_MODEL, bias=v1(V_LNEPS)).then_inc(ln_act, 1)

        @block.vector
        def _(dve):
            def lo(n, slot):
                dve.wait_ge(split_hi, n + 1)
                dve.tensor_tensor(wlo[:, slot, :], wraw[:, slot, :], whi[:, slot, :].bitcast(F32),
                                  ALU.subtract).then_inc(split_lo, 1)

            def lo_step(n0, k):
                lo(n0 + k + LEAD, (k + LEAD) % RING)

            stt = dve.scalar_tensor_tensor
            tt = dve.tensor_tensor

            dve.memset(xp[:], 0.0).then_inc(conv_done, 1)
            dve.memset(cv[:], 0.0).then_inc(conv_done, 1)
            for j, s in enumerate((x_in0, x_in1)):
                dve.wait_ge(s, 16)
                dve.tensor_copy(xh[:, 4 * j:4 * j + 4, :], x0[:, 4 * j:4 * j + 4, :]).then_inc(x_split, 1)
            for j in range(2):
                c = slice(4 * j, 4 * j + 4)
                dve.wait_ge(x_split, j + 1)
                tt(xl[:, c, :], x0[:, c, :], xh[:, c, :].bitcast(F32), ALU.subtract).then_inc(x_split, 1)
            for n in range(LEAD):
                lo(n, n)

            dve.wait_ge(in_loaded, 64)
            step = [0]

            def link(ins):
                step[0] += 1
                ins.then_inc(m_dve, 1)
                dve.wait_ge(m_dve, step[0])

            dve.wait_ge(misc_done, 1)
            dve.tensor_copy(kt[:, 0, :], ps_ss[0:32, 0:T])
            dve.tensor_copy(kt[:, 1, :], ps_ss[32:64, 0:T])
            link(dve.tensor_copy(dt_r[:], ps_ss[64:96, 0:T]))
            link(dve.tensor_scalar(dt_r[:], dt_r[:], vec[0:32, V_DTB:V_DTB + 1], None, ALU.add))
            stt(dt_a[:], dt_r[:], -1.0, dt_r[:], ALU.mult, ALU.min).then_inc(dt_pre, 1)
            c32, s32 = cos[0:32, :], sin[0:32, :]
            tt(kt[:, 2, :], kt[:, 0, :], c32, ALU.mult)
            link(tt(kt[:, 3, :], kt[:, 1, :], s32, ALU.mult))
            tt(krot[:, 0, :], kt[:, 2, :], kt[:, 3, :], ALU.subtract).then_inc(krot_done, 1)
            dve.wait_ge(krot_done, 1)
            tt(kt[:, 2, :], kt[:, 0, :], s32, ALU.mult)
            link(tt(kt[:, 3, :], kt[:, 1, :], c32, ALU.mult))
            tt(krot[:, 1, :], kt[:, 2, :], kt[:, 3, :], ALU.add).then_inc(krot_done, 1)
            dve.wait_ge(m_act, 2)
            link(stt(dt_v[:], dt_r[:], 0.0, dt_a[:], ALU.max, ALU.add))
            dve.wait_ge(m_act, 3)
            link(dve.tensor_scalar(dta[:], dt_v[:], small[:, 0:1], -1.0, ALU.mult, ALU.mult))
            dve.tensor_tensor_scan(acum[:, 0:SEQ], one_row[:, 0:SEQ], dta[:, 0:SEQ], 0.0, ALU.mult,
                                   ALU.add).then_inc(acum_ready, 1)
            dve.tensor_tensor_scan(acum[:, SEQ:T], one_row[:, SEQ:T], dta[:, SEQ:T], 0.0, ALU.mult,
                                   ALU.add).then_inc(acum_ready, 1)
            dve.wait_ge(acum_ready, 2)
            link(dve.tensor_copy(acum_h[:], acum[:]))
            tt(acum_l[:], acum[:], acum_h[:].bitcast(F32), ALU.subtract).then_inc(mid_done, 1)
            dve.wait_ge(m_act, 6)
            dve.tensor_scalar(dend[:], ident[0:32, 0:32], small[:, 1:2], None, ALU.mult).then_inc(dend_ready, 1)
            dve.wait_ge(krot_done, 2)
            for q in range(4):
                dve.tensor_copy(kpr[32 * q:32 * q + 32, :], krot[:, q % 2, :])
            dve.tensor_copy(ones_r[:], con[0:HEADS_SSM, C_ONE:C_ONE + P]).then_inc(mid_done, 1)
            dve.wait_ge(mid_done, 2)
            dve.tensor_copy(kpall[:, PAST:KEYS], kpr[:, SEQ:T])
            with dve.Fori(0, CB // 4) as i:
                for k in range(4):
                    b, u = 4 * i + k, k % 2
                    lo_step(4 * i, k)
                    dve.wait_ge(tap3_done, b + 1)
                    for tap in range(3):
                        if tap:
                            dve.wait_ge(tap_chain, 2 * b + tap)
                        stt(cv[:, u, :], xp[:, u, 1 + tap:1 + tap + CW], vd(V_CONVW + tap * CB + b), cv[:, u, :],
                            ALU.mult, ALU.add).then_inc(tap_chain if tap < 2 else conv_done, 1)

            dve.wait_ge(m_pe, 1)
            dve.tensor_copy(tokv[:, 0:2, :, :].rearrange("p t k h -> p (t k h)"), ps_tr[:, 0:192])
            dve.tensor_copy(tokv[0:32, 2, :, :].rearrange("p k h -> p (k h)"), ps_tr[0:32, 192:288])
            dve.tensor_copy(dec_b[:], ps_cb[:, 0:HEADS_SSM]).then_inc(mid_done, 1)
            dve.wait_ge(mid_done, 3)
            dve.wait_ge(silu_done, CB + 1)

            with dve.Fori(0, GROUPS // 2) as i:
                for p in range(2):
                    g = 2 * i + p
                    n0 = N_SSD + 4 * g
                    step[0] = 0

                    def link3(ins):
                        step[0] += 1
                        ins.then_inc(d3, 1)
                        return 7 * g + step[0]

                    def wait3(count):
                        dve.wait_ge(d3, count)

                    def heads(rows, t, kind, free):
                        return tokv[0:rows, t, kind, bass.ds(4 * g, 4)].unsqueeze(2).to_broadcast([rows, HPG, free])

                    def tokens(t):
                        n = P if t < 2 else DEC_SEQ
                        dve.wait_ge(tr_done, 3 * g + t + 1)
                        d = link3(tt(xdt[0:n, t, :].rearrange("p (h d) -> p h d", h=HPG),
                                     ps_tr[0:n, 0:2 * P].rearrange("p (h d) -> p h d", h=HPG),
                                     heads(n, t, 0, 64), ALU.mult))
                        dve.tensor_copy(btok[0:n, t, :], ps_tr[0:n, 2 * P:3 * P]).then_inc(tr_free, 1)
                        return d

                    def decayed(t, d):
                        n = P if t < 2 else DEC_SEQ
                        wait3(d)
                        tt(wx[0:n, t, :].rearrange("p (h d) -> p h d", h=HPG),
                           xdt[0:n, t, :].rearrange("p (h d) -> p h d", h=HPG),
                           heads(n, t, 2, 64), ALU.mult).then_inc(wx_done, 1)

                    lo_step(n0, 0)
                    dve.wait_ge(rows_done, g + 2)
                    for t in range(2):
                        for h4 in range(HPG):
                            c = (h4 % 2) * SEQ + t * P
                            stt(seg[:, 2 * t, h4, :], ps_row[:, h4 // 2, c:c + P],
                                tokv[:, t, 1, bass.ds(4 * g + h4, 1)], tri, ALU.subtract, ALU.min)
                    tt(seg[:, 1, :, :].rearrange("p (r h) i -> p r h i", r=2),
                       ps_row[:].rearrange("p r (h i) -> p r h i", h=2)[:, :, :, P:SEQ],
                       tokv[:, 0, 1, bass.ds(4 * g, 4)].rearrange("p (r h) -> p r h", r=2).unsqueeze(3)
                       .to_broadcast([P, 2, 2, P]), ALU.subtract)
                    d = link3(tt(segs[:], ps_ss[0:DEC_SEQ, 384:512].rearrange("p (h i) -> p h i", h=HPG),
                                 heads(DEC_SEQ, 2, 1, DEC_SEQ), ALU.subtract))
                    wait3(d)
                    tt(segs[:], segs[:], tri[0:DEC_SEQ, 0:DEC_SEQ].unsqueeze(1).to_broadcast([DEC_SEQ, HPG, DEC_SEQ]),
                       ALU.min).then_inc(seg_done, 1)
                    d0 = tokens(0)
                    lo_step(n0, 1)
                    decayed(0, d0)
                    d1 = tokens(1)
                    dve.wait_ge(exp_done, g + 1)
                    dve.wait_ge(cb_done, g + 1)
                    d = link3(tt(seg[:], seg[:], ps_cb[:, 0:384].rearrange("p (a i) -> p a i", a=3).unsqueeze(2)
                                 .to_broadcast([P, 3, HPG, P]), ALU.mult))
                    tt(segs[:], segs[:], ps_cb[0:DEC_SEQ, 384:384 + DEC_SEQ].unsqueeze(1)
                       .to_broadcast([DEC_SEQ, HPG, DEC_SEQ]), ALU.mult).then_inc(m_done, 1)
                    tt(c_dec[:], e_row[:], xcg[:, p, 3, SC:CW].unsqueeze(1).to_broadcast([P, HPG, DEC_SEQ]),
                       ALU.mult).then_inc(c_done, 1)
                    lo_step(n0, 2)
                    decayed(1, d1)
                    d2 = tokens(2)
                    decayed(2, d2)
                    dve.wait_ge(state_in[p], 16 * (i + 1))
                    sd = link3(tt(s_dec[:].rearrange("p (h d) -> p h d", h=HPG),
                                  s_in[:, p, :].rearrange("p (h d) -> p h d", h=HPG),
                                  dec_b[:, bass.ds(4 * g, 4)].unsqueeze(2).to_broadcast([P, HPG, 64]), ALU.mult))
                    lo_step(n0, 3)
                    dve.wait_ge(y_done, g + 1)
                    for q in range(2):
                        d_skip = vd(V_D + 2 * g + q)
                        stt(ysb[:, q, 0:SEQ], xcg[:, p, q, 0:SEQ], d_skip, ps_row[:, q, 0:SEQ], ALU.mult, ALU.add)
                        y = stt(ysb[:, q, SEQ:T], xcg[:, p, q, SC:CW], d_skip, ps_row[:, q, SEQ:T],
                                ALU.mult, ALU.add)
                    y.then_inc(y_free, 1)
                    dve.wait_ge(y_free, g + 2)
                    dve.wait_ge(freed_act, F_SSD + 4 * g + 4)
                    tt(xc[:, bass.ds(2 * g + 1, 2), 0:T], ysb[:], zt[:], ALU.mult).then_inc(yz_done, 1)
                    dve.wait_ge(s_done, g + 1)
                    dve.wait_ge(s_stored[p], 32 * i + 1)
                    link3(dve.tensor_copy(s_out[:, p, 0, :], ps_s[:, 0:2 * P]))
                    wait3(sd)
                    tt(s_out[:, p, 1, :], s_dec[:], ps_s[:, 2 * P:4 * P], ALU.add).then_inc(s_ready, 1)
                    assert step[0] == 7

            with dve.Fori(0, 2) as i:
                for k in range(4):
                    j = 4 * i + k
                    lo_step(N_QKV + 4 * i, k)
                    dve.wait_ge(std_done, j + 1)
                    dve.reciprocal(blk(var_s, j), blk(var_s, j)).then_inc(rstd_done, 1)
                    for s in s_stored:
                        dve.wait_ge(s, 16 * GROUPS + 1)
                    dve.wait_ge(rstd_done, j + 1)
                    dve.wait_ge(norm_done, j + 1)
                    for q in range(2):
                        y = stt(yt[:, q, :], xc[:, bass.ds(2 * j + 1 + q, 1), 0:T].rearrange("p a b -> p (a b)"),
                                vd(V_SSMG + 2 * j + q), blk(var_s, j), ALU.mult, ALU.mult)
                    y.then_inc(norm_t, 1)
                    dve.wait_ge(norm_h, j + 1)
                    tt(yn_l[:, bass.ds(2 * j, 2), :], yt[:], yn_h[:, bass.ds(2 * j, 2), :].bitcast(F32),
                       ALU.subtract).then_inc(norm_done, 1)

            dve.wait_ge(lat_std, 2)
            dve.reciprocal(rqk[:], rqk[:]).then_inc(lat_dve, 1)
            dve.wait_ge(lat_dve, 1)
            for k in range(RB):
                stt(ckvn[:, k, :], qk[:, RB + k, :], v1(V_KVG + k), rqk[:, 1, :], ALU.mult, ALU.mult)
            for k in range(RB):
                y = stt(qn[:, k, :], qk[:, k, :], v1(V_QG + k), rqk[:, 0, :], ALU.mult, ALU.mult)
            y.then_inc(lat_dve, 1)
            dve.wait_ge(lat_done, 1)
            tt(q_l[:], qn[:], q_h[:].bitcast(F32), ALU.subtract).then_inc(lat_dve, 1)
            dve.wait_ge(lat_done, 2)
            tt(ckv_l[:], ckvn[:], ckv_h[:].bitcast(F32), ALU.subtract).then_inc(lat_dve, 1)
            dve.tensor_copy(ckvT[:, :, PAST:KEYS], ckvn[:, :, SEQ:T]).then_inc(tok_cp, 1)

            def gate_phase(n0, mla):
                with dve.Fori(0, KB // 2) as i:
                    for j in range(2):
                        b = 2 * i + j
                        lo_step(n0 + 4 * i, 2 * j)
                        lo_step(n0 + 4 * i, 2 * j + 1) if not mla else None
                        dve.wait_ge(sig_done, (KB if mla else 0) + b + 1)
                        dve.wait_ge(chunk_used, n0 + 4 * i + 2 * j + 3)
                        if not mla:
                            tt(blk(ssmg, b), ps_acc[:, j, 0:T], sig[:, j, :], ALU.mult).then_inc(freed_dve, 1)
                        else:
                            tt(mixt[:, j, :], ps_acc[:, j, 0:T], sig[:, j, :], ALU.mult).then_inc(freed_dve, 1)
                            dve.wait_ge(freed_dve, G_MLA + b + 3)
                            tt(mixt[:, j, :], mixt[:, j, :], blk(ssmg, b), ALU.add).then_inc(mix_t, 1)
                            lo_step(n0 + 4 * i, 2 * j + 1)
                            dve.wait_ge(mix_hi, b + 1)
                            tt(blk(mix_l, b), mixt[:, j, :], blk(mix_h, b).bitcast(F32),
                               ALU.subtract).then_inc(mix_lo, 1)

            gate_phase(N_SSM, False)
            dve.wait_ge(tok_pe, 1)
            dve.tensor_copy(ckvK[0:DEC_SEQ, 4, :], ps_tr[0:DEC_SEQ, :]).then_inc(tok_cp, 1)

            dve.memset(qz[:], 0.0).then_inc(d5, 1)
            dve.wait_ge(d5, 1)
            with dve.Fori(0, ROUNDS) as i:
                n0 = N_ATT + ATT_CHUNKS * i
                f0 = F_ATT + ATT_TURNS * i
                step[0] = 0

                def link5(ins):
                    step[0] += 1
                    ins.then_inc(d5, 1)
                    dve.wait_ge(d5, 6 * i + step[0] + 1)

                for k in range(4):
                    lo_step(n0, k)
                dve.wait_ge(freed_act, f0 + 6 + 2)
                tt(rope_t[:, 0, :], qab[:, 0, :], cos, ALU.mult)
                tt(rope_t[:, 1, :], qab[:, 1, :], sin, ALU.mult)
                tt(rope_t[:, 2, :], qab[:, 0, :], sin, ALU.mult)
                link5(tt(rope_t[:, 3, :], qab[:, 1, :], cos, ALU.mult))
                for h4 in range(4):
                    src = slice(32 * h4, 32 * h4 + 32)
                    for half in range(2):
                        o = 64 * (h4 % 2) + 32 * half
                        y = tt(pe2[o:o + 32, h4 // 2, :], rope_t[src, 2 * half, :], rope_t[src, 2 * half + 1, :],
                               ALU.add if half else ALU.subtract)
                link5(y)
                dve.tensor_copy(qz[0:64, 0:4:2, :], pe2[0:64, :, SEQ:T])
                dve.tensor_copy(qz[64:P, 1:4:2, :], pe2[64:P, :, SEQ:T]).then_inc(pe_done, 1)
                lo_step(n0, 4)
                dve.wait_ge(qlat_done, 4 * i + 4 + 2)
                dve.tensor_copy(qlat[:].rearrange("p c q -> p (c q)"), ps_s[:]).then_inc(qlat_cp, 1)
                for h4 in range(4):
                    dve.wait_ge(sc_done, 4 * i + h4 + 1)
                    y = stt(prob[:, h4, :], ps_att[h4][:, 0:384], SCALE, mask, ALU.mult, ALU.add)
                y.then_inc(sc_evac, 1)
                dve.wait_ge(sc_evac, i + 1)
                dve.tensor_reduce(stat[:, 0, 0:4], prob[:, :, 0:P], AX, ALU.max)
                link5(dve.tensor_reduce(stat[:, 0, 4:8], prob[:, :, P:384], AX, ALU.max))
                dve.tensor_scalar(stat[:, 1, 0:8], stat[:, 0, 0:8], -1.0, None, ALU.mult).then_inc(amax, 1)
                lo_step(n0, 5)
                dve.wait_ge(ssc_done, i + 1)
                dve.tensor_scalar(ssc[:, 0:PAST], ps_s[:], SCALE, None, ALU.mult)
                link5(dve.tensor_scalar(ssc[:, PAST:KEYS], ps_ss[:, 0:DEC_SEQ], SCALE, None, ALU.mult))
                link5(dve.tensor_reduce(stat[:, 0, 8:9], ssc[:], AX, ALU.max))
                dve.tensor_scalar(stat[:, 1, 8:9], stat[:, 0, 8:9], -1.0, None, ALU.mult).then_inc(samax, 1)
                dve.wait_ge(aexp, i + 1)
                link5(dve.reciprocal(stat[:, 3, 0:8], stat[:, 2, 0:8]))
                for h4 in range(4):
                    for q, (a, b) in enumerate(((0, P), (P, 384))):
                        y = dve.tensor_scalar(prob[:, h4, a:b], prob[:, h4, a:b],
                                              stat[:, 3, 4 * q + h4:4 * q + h4 + 1], None, ALU.mult)
                y.then_inc(anorm, 1)
                dve.wait_ge(saexp, i + 1)
                dve.reciprocal(stat[:, 3, 8:9], stat[:, 2, 8:9]).then_inc(ssc_rec, 1)
                dve.wait_ge(ssc_rec, i + 1)
                dve.tensor_scalar(ssc[:], ssc[:], stat[:, 3, 8:9], None, ALU.mult).then_inc(anorm, 1)
                lo_step(n0, 6)
                dve.wait_ge(st_done, i + 1)
                dve.tensor_copy(ssT[:, 0:4, :].rearrange("p c q -> p (c q)"), ps_s[:])
                dve.tensor_copy(ssT[0:DEC_SEQ, 4, :], ps_ss[0:DEC_SEQ, 0:P]).then_inc(st_cp, 1)
                dve.wait_ge(ol_hi, i + 1)
                tt(olat_l[:].rearrange("p c q -> p (c q)"), ps_s[:],
                   olat_h[:].rearrange("p c q -> p (c q)").bitcast(F32), ALU.subtract).then_inc(ol_lo, 1)
                dve.wait_ge(o_hi, i + 1)
                tt(o_l[:, bass.ds(4 * i, 4), :], of[:], o_h[:, bass.ds(4 * i, 4), :].bitcast(F32),
                   ALU.subtract).then_inc(o_lo, 1)
                lo_step(n0, 7)
                assert step[0] == 6

            gate_phase(N_MLA, True)

            dve.wait_ge(xr_loaded, 16)
            dve.memset(mean[:, 1, :], 0.0).then_inc(ln_sum, 1)
            with dve.Fori(0, 2) as i:
                for k in range(4):
                    lo_step(N_OUT + 4 * i, k)
                    dve.wait_ge(chunk_used, N_OUT + 4 * i + k + 2)
                    stt(blk(hp, 4 * i + k), blk(xr, 4 * i + k), ALPHA, ps_acc[:, k % 2, 0:T], ALU.mult,
                        ALU.add).then_inc(freed_dve, 1)
                    dve.wait_ge(freed_dve, G_OUT + 4 * i + k + 3)
                    dve.wait_ge(ln_sum, 4 * i + k + 1)
                    tt(mean[:, 1, :], mean[:, 1, :], blk(hp, 4 * i + k), ALU.add).then_inc(ln_sum, 1)

            def layer_norm(t, m, out, gcol, bcol, done, sums):
                def wide(x):
                    return x.unsqueeze(1).to_broadcast([P, KB // 2, T])
                dve.wait_ge(ln_pe, sums + 1)
                dve.tensor_scalar(m[:, 0, :], ps_s[:, 0:T], 1.0 / D_MODEL, None, ALU.mult).then_inc(ln_dve, 1)
                dve.wait_ge(ln_dve, done + 1)
                halves = (slice(0, 4), slice(4, 8))
                for c in halves:
                    tt(t[:, c, :], t[:, c, :], wide(m[:, 0, :]), ALU.subtract).then_inc(ln_dve, 1)
                dve.wait_ge(ln_act, 3 if not done else 8)
                dve.reciprocal(m[:, 2, :], m[:, 1, :]).then_inc(ln_dve, 1)
                dve.wait_ge(ln_dve, done + 4)
                for c in halves:
                    tt(t[:, c, :], t[:, c, :], wide(m[:, 2, :]), ALU.mult).then_inc(ln_dve, 1)
                for q in range(2):
                    dve.wait_ge(ln_dve, done + 5 + q)
                    for k in range(4 * q, 4 * q + 4):
                        y = dve.tensor_scalar(out[:, k, :], t[:, k, :], v1(gcol + k), v1(bcol + k), ALU.mult, ALU.add)
                    y.then_inc(ln_dve, 1)

            layer_norm(hp, mean, h, V_LN1G, V_LN1B, 0, 0)
            for q in range(2):
                c = slice(4 * q, 4 * q + 4)
                dve.wait_ge(ln_act, 4 + q)
                tt(h_l[:, c, :], h[:, c, :], h_h[:, c, :].bitcast(F32), ALU.subtract).then_inc(ln_dve, 1)

            with dve.Fori(0, FB // 4) as i:
                for k in range(4):
                    b, u = 4 * i + k, k % 2
                    lo_step(N_UP + 4 * i, k)
                    dve.wait_ge(freed_act, F_UP + b + 3)
                    tt(ff[:, u, :], rl[:, u, :], rl[:, u, :], ALU.mult).then_inc(ff_sq, 1)
                    dve.wait_ge(ff_hi, b + 1)
                    tt(blk(ff_l, b), ff[:, u, :], blk(ff_h, b).bitcast(F32), ALU.subtract).then_inc(ff_lo, 1)

            def down(b, u, splits):
                for k in range(splits):
                    lo_step(N_DOWN + 4 * b, k)
                dve.wait_ge(chunk_used, N_DOWN + 4 * b + 5)
                stt(blk(yp, b), blk(h, b), ALPHA, ps_acc[:, u, 0:T], ALU.mult, ALU.add).then_inc(freed_dve, 1)
                dve.wait_ge(freed_dve, G_DOWN + b + 3)
                dve.wait_ge(ln_sum, KB + b + 2)
                tt(lnm[:, 1, :], lnm[:, 1, :], blk(yp, b), ALU.add).then_inc(ln_sum, 1)

            dve.memset(lnm[:, 1, :], 0.0).then_inc(ln_sum, 1)
            with dve.Fori(0, KB // 2 - 1) as i:
                down(2 * i, 0, 4)
                down(2 * i + 1, 1, 4)
            down(KB - 2, 0, 4)
            down(KB - 1, 1, 1)
            layer_norm(yp, lnm, yp, V_LN2G, V_LN2B, 10, 2)

        @block.gpsimd
        def _(pool):
            for o in (0, 64):
                pool.dma_start(kpall[o:o + 64, 0:PAST], kpeT).then_inc(late_loaded, 16)
            pool.wait_ge(in_loaded, 64)
            with pool.Fori(0, CB // 4) as i:
                for k in range(4):
                    b, u = 4 * i + k, k % 2
                    pool.wait_ge(conv_done, b + 1)
                    pool.tensor_copy(xp[:, u, 261:264], blk(cstate, b)).then_inc(xp_state, 1)
                    pool.wait_ge(freed_act, b + 3)
                    pool.tensor_copy(blk(cnew, b).rearrange("p (a c) -> p a c", a=2),
                                     xp[:, u, 8:XW].rearrange("p (a c) -> p a c", c=36)[:, 6:8, 33:36]
                                     ).then_inc(xp_saved, 1)
            pool.wait_ge(xp_saved, CB + 2)
            pool.dma_start(o_conv, cnew[:]).then_inc(conv_out, 16)
            pool.wait_ge(mid_done, 3)
            pool.wait_ge(stored, 16)

            def rows(g):
                pool.wait_ge(rows_done, g + 1)
                pick = ident[0:HEADS_SSM, bass.ds(4 * g, 4)].unsqueeze(2).to_broadcast([HEADS_SSM, HPG, T])
                for out, src in ((rows_h, acum_h), (rows_l, acum_l)):
                    pool.tensor_tensor(out[:], src[:].bitcast(F32).unsqueeze(1).to_broadcast([HEADS_SSM, HPG, T]),
                                       pick, ALU.mult).then_inc(rows_made, 1)

            with pool.Fori(0, GROUPS // 2) as i:
                for p in range(2):
                    g = 2 * i + p
                    rows(g)
                    pool.wait_ge(silu_done, CB + 1)
                    pool.wait_ge(yz_done, g + 1)
                    pool.tensor_copy(xcg[:, p, 0:2, :], xc[:, bass.ds(2 * g + 1, 2), :]).then_inc(staged, 1)
                    pool.tensor_copy(xcg[:, p, 2, :], blk(xc, XB + 1 + g)).then_inc(staged, 1)
                    pool.tensor_copy(xcg[:, p, 3, :], blk(xc, XB + GROUPS + 1 + g)).then_inc(staged, 1)
                    pool.wait_ge(conv_out, 16)
                    pool.dma_start(s_in[:, p, :], stateS[bass.ds(g, 1)].rearrange("a p c -> (a p) c")
                                   ).then_inc(state_in[p], 16)
            rows(GROUPS)
            pool.wait_ge(norm_done, GROUPS + 1)
            pool.dma_start(ckvT[:, :, 0:PAST], cacheT).then_inc(late_loaded, 16)
            pool.dma_start(ckvK[:, 0:4, :], cacheK).then_inc(late_loaded, 16)
            with pool.Fori(0, ROUNDS) as i:
                for h4 in range(4):
                    pool.wait_ge(qlat_done, 4 * i + h4 + 1)
                    pool.dma_start(side[:, h4 % 2, :], ukT[bass.ds(4 * i + h4, 1)].rearrange("a p c -> (a p) c")
                                   ).then_inc(side_in[h4 % 2], 16)
            pool.wait_ge(chunk_used, N_MLA + 1)
            pool.wait_ge(o_lo, ROUNDS)
            pool.dma_start(xr[:], xT).then_inc(xr_loaded, 16)


def _constants(np):
    con = np.zeros((P, C_ALL), np.float32)
    con[:, C_ID:C_ID + P] = np.eye(P)
    con[:, C_ONE:C_TRI] = 1.0
    r = np.arange(P)
    con[:, C_TRI:C_TRI + P] = np.where(r[:, None] <= r[None, :], 0.0, -1e30)
    m = np.where(r[None, :] // CHUNK <= r[:, None] // CHUNK, 0.0, -1e30)
    con[:, C_MASK:C_MASK + P] = m
    con[:, C_MASK + 2 * P:C_MASK + 3 * P] = m
    inv = np.float32(10000.0) ** (-np.arange(0, ROPE, 2, dtype=np.float32) / np.float32(ROPE))
    pos = np.concatenate([np.arange(SEQ), PAST + np.arange(DEC_SEQ)]).astype(np.float32)
    ang = (inv[:, None] * pos[None, :]).astype(np.float32)
    con[:, C_COS:C_COS + T] = np.tile(np.cos(ang), (4, 1))
    con[:, C_SIN:C_SIN + T] = np.tile(np.sin(ang), (4, 1))
    return con


def _layout(x, np):
    f = {k: np.asarray(v)[0] for k, v in x.items()}
    xT = np.concatenate([f["x_prompt"], f["x_sample"]], 0).T

    def feat(v):
        return v.reshape(-1, P).T

    def blocks(w):
        k, m = w.shape
        return w.reshape(k // P, P, m // P, P).transpose(2, 1, 0, 3)

    w = f["w_in"]
    c = [0, 2 * D_MODEL, 2 * D_MODEL + D_INNER]
    c += [c[2] + CONV_DIM, c[2] + CONV_DIM + HEADS_SSM]
    c += [c[4] + RANK, c[4] + 2 * RANK, c[4] + 2 * RANK + ROPE]
    gate, z, xbc, dt, q_a, ckv, kpe = (w[:, a:b] for a, b in zip(c, c[1:]))
    parts = [blocks(xbc).reshape(CB, P, CK)]
    zb, gb = blocks(z).reshape(-1, 1, 2, P, CK), blocks(gate).reshape(-1, 1, 2, P, CK)
    parts.append(np.concatenate([zb.reshape(GROUPS, 2, P, CK), gb.reshape(GROUPS, 2, P, CK)], 1).reshape(-1, P, CK))
    parts.append(blocks(q_a).reshape(RB, P, CK))
    parts.append(blocks(ckv).reshape(RB, P, CK))

    def deep(w):
        b = blocks(w)
        m, _, k, _ = b.shape
        return b.reshape(m, P, k // 8, 8 * P).transpose(0, 2, 1, 3).reshape(-1, P, CK)

    parts.append(deep(f["w_ssm_proj"]))
    qb = f["w_q_b"].reshape(RANK, HEADS, NOPE + ROPE)
    uk, uv = f["w_uk"], f["w_uv"]
    for r in range(ROUNDS):
        hs = slice(4 * r, 4 * r + 4)
        b = [qb[:, 4 * r + j, :NOPE] for j in range(4)]
        b += [qb[:, hs, NOPE:NOPE + HALF].reshape(RANK, P), qb[:, hs, NOPE + HALF:].reshape(RANK, P)]
        b += [uk[:, 4 * r + j] for j in range(4)]
        b = blocks(np.concatenate(b, 1)).reshape(5, 2, P, RB * P).transpose(0, 2, 1, 3).reshape(5, P, CK)
        v = uv[:, hs].reshape(RB, P, 2, 2 * P).transpose(2, 1, 0, 3).reshape(2, P, CK)
        parts += [b, np.zeros((1, P, CK), np.float32), v]
    parts += [deep(f["w_mla_proj"]), blocks(f["w_out"]).reshape(KB, P, CK),
              blocks(f["w_up"]).reshape(FB, P, CK), deep(f["w_down"])]
    wst = np.concatenate(parts, 0)
    assert wst.shape == (N_ALL, P, CK), wst.shape
    misc = np.concatenate([kpe, dt], 1).reshape(KB, P, 96).transpose(1, 0, 2)
    vecs = np.zeros((P, V_ALL), np.float32)
    cw = f["conv_w"].reshape(4, CB, P)
    vecs[:, V_CONVW:V_CONVB] = cw.reshape(4 * CB, P).T
    for col, name in ((V_CONVB, "conv_b"), (V_GATE, "b_gate"), (V_SSMG, "ssm_norm_g"), (V_QG, "q_norm_g"),
                      (V_KVG, "kv_norm_g"), (V_LN1G, "ln1_g"), (V_LN1B, "ln1_b"), (V_LN2G, "ln2_g"),
                      (V_LN2B, "ln2_b")):
        v = feat(f[name])
        vecs[:, col:col + v.shape[1]] = v
    vecs[:, V_D:V_D + XB] = np.repeat(f["d_skip"], 64).reshape(XB, P).T
    vecs[0:HEADS_SSM, V_DTB] = f["dt_bias"]
    vecs[0:HEADS_SSM, V_ALOG] = f["a_log"]
    vecs[:, V_EPS] = RMS_EPS
    vecs[:, V_LNEPS] = LN_EPS
    cache = f["cache_ckv"][0]
    return dict(
        wst=wst, xT=xT.reshape(KB, P, T).transpose(1, 0, 2), misc=misc, vecs=vecs, consts=_constants(np),
        ukT=uk.transpose(1, 2, 0), cacheT=cache.T.reshape(RB, P, PAST).transpose(1, 0, 2),
        cacheK=cache.reshape(4, P, RANK).transpose(1, 0, 2), kpeT=f["cache_kpe"][0].T,
        stateS=f["state_ssm"][0].reshape(GROUPS, HPG * 64, STATE).transpose(0, 2, 1),
        stateC=f["state_conv"][0].reshape(3, CB, P).transpose(2, 1, 0),
    )


_INS = ["wst", "xT", "misc", "vecs", "consts", "ukT", "cacheT", "cacheK", "kpeT", "stateS", "stateC"]
_OUTS = {"y": (P, KB, T), "ckv": (P, RB, T), "kpe": (HALF, 2, T), "ssm": (2, GROUPS, P, 2 * P),
         "conv": (P, CB, 6)}


def kernel(**inputs):
    import numpy as np
    import concourse.bacc as bacc
    from concourse.bass_utils import run_bass_kernel_spmd as run

    nc = bacc.Bacc("TRN2", target_bir_lowering=False, num_devices=1)
    laid = _layout(inputs, np)
    arrays = {f"in_{k}": np.ascontiguousarray(laid[k]) for k in _INS}
    args = [nc.dram_tensor(k, a.shape, F32, kind="ExternalInput").ap() for k, a in arrays.items()]
    args += [nc.dram_tensor(f"out_{k}", s, F32, kind="ExternalOutput").ap() for k, s in _OUTS.items()]
    layer_program(nc, *args)
    r = run(nc, [arrays], core_ids=[0]).results[0]

    def frames(name):
        a = np.asarray(r[f"out_{name}"])
        return a.transpose(2, 1, 0).reshape(T, -1)

    y, ckv = frames("y"), frames("ckv")
    kpe = np.asarray(r["out_kpe"]).transpose(2, 1, 0).reshape(T, ROPE)
    ssm = np.asarray(r["out_ssm"]).transpose(0, 1, 3, 2).reshape(2, HEADS_SSM, 64, STATE)
    conv = np.asarray(r["out_conv"]).reshape(P, CB, 2, 3).transpose(2, 3, 1, 0).reshape(2, 3, CONV_DIM)
    return (y[:SEQ][None], y[SEQ:][None], ckv[:SEQ][None, None], kpe[:SEQ][None, None],
            ssm[0][None, None], conv[0][None, None], ckv[SEQ:][None, None], kpe[SEQ:][None, None],
            ssm[1][None, None], conv[1][None, None])
```
